# Optimizing a Trainium2 kernel written in Bass

```python
import jax, jax.numpy as jnp
from jax import lax
import numpy as np

D_MODEL = 1024
BATCH = 1
SEQ = 256
DEPTH = 2

CTX_LEN = 256
GRID_W = 64
NORM_EPS = 1e-6
POOL_WIDTH = 1024
POOL_WINDOWS = (2, 4, 8, 16)
POOL_GROUP = POOL_WIDTH // len(POOL_WINDOWS)
GLA_HEADS = 4
GLA_DK = 128
GLA_DV = 256
GLA_GATE_RANK = 16
GLA_TAU = 16.0
GLA_CHUNK = 64
MLA_HEADS = 8
MLA_Q_RANK = 384
MLA_KV_RANK = 256
MLA_NOPE = 128
MLA_ROPE = 64
MLA_V = 128
ROPE_BASE = 10000.0
Q_BLOCK = 128
N_BRANCH = 3
BRANCH_WIDTH = 1024
PEER_HEADS = 8
PEER_N_KEYS = 128
PEER_N_EXPERTS = PEER_N_KEYS * PEER_N_KEYS
PEER_TOPK = 16
PEER_QDIM = 256
PEER_HALF = PEER_QDIM // 2
PEER_BLOCK = 128
IN_SPLITS = (POOL_WIDTH, GLA_HEADS * GLA_DK, GLA_HEADS * GLA_DK, GLA_HEADS * GLA_DV, GLA_HEADS * GLA_DV,
             GLA_GATE_RANK, GLA_GATE_RANK, MLA_Q_RANK, MLA_KV_RANK, MLA_ROPE, N_BRANCH * D_MODEL)
IN_COLS = sum(IN_SPLITS)

kernel_name = "hybrid_pool_gla_mla_peer_diffusion_block"

F32 = jnp.float32

def rmsnorm(x, g):
    xf = x.astype(F32)
    y = xf * lax.rsqrt(jnp.mean(xf * xf, axis=-1, keepdims=True) + NORM_EPS)
    return (y * g.astype(F32)).astype(x.dtype)

def split_cols(z):
    idx, acc = [], 0
    for s in IN_SPLITS[:-1]:
        acc += s
        idx.append(acc)
    return jnp.split(z, idx, axis=-1)

def flip(a):
    return jnp.flip(a, axis=1)

def axial_angles(T):
    n_rows = T // GRID_W
    row = jnp.repeat(jnp.arange(n_rows), GRID_W).astype(F32)
    col = jnp.tile(jnp.arange(GRID_W), n_rows).astype(F32)
    half = MLA_ROPE // 2
    inv = ROPE_BASE ** (-jnp.arange(0, half, 2, dtype=F32) / half)
    return row[:, None] * inv, col[:, None] * inv

def rotate(x, ang):
    m = x.shape[-1] // 2
    x1, x2 = x[..., :m], x[..., m:]
    cos, sin = jnp.cos(ang).astype(x.dtype), jnp.sin(ang).astype(x.dtype)
    return jnp.concatenate([x1 * cos - x2 * sin, x1 * sin + x2 * cos], axis=-1)

def axial_rope(x, ang_row, ang_col):
    h = x.shape[-1] // 2
    return jnp.concatenate([rotate(x[..., :h], ang_row), rotate(x[..., h:], ang_col)], axis=-1)

def multiscale_pool(u, w, scale):
    T = u.shape[1]
    uf = u.astype(F32)
    cs = jnp.concatenate([jnp.zeros_like(uf[:, :1]), jnp.cumsum(uf, axis=1)], axis=1)
    t = jnp.arange(T)
    outs = []
    for gi, win in enumerate(POOL_WINDOWS):
        lo = jnp.clip(t - win // 2, 0, T)
        hi = jnp.clip(t + win - win // 2, 0, T)
        sl = slice(gi * POOL_GROUP, (gi + 1) * POOL_GROUP)
        csg = cs[..., sl]
        mean = (csg[:, hi] - csg[:, lo]) / (hi - lo).astype(F32)[:, None]
        diff = (mean - uf[..., sl]).astype(u.dtype)
        outs.append(diff @ w[gi])
    return jnp.concatenate(outs, axis=-1) * scale

def gla_chunk_scan(q, k, v, g, s0):
    Bn, T, H, _ = q.shape
    dv = v.shape[-1]
    n = T // GLA_CHUNK

    def to_chunks(a):
        return a.astype(F32).reshape(Bn, n, GLA_CHUNK, H, a.shape[-1]).transpose(1, 0, 3, 2, 4)

    mask = jnp.tril(jnp.ones((GLA_CHUNK, GLA_CHUNK), dtype=bool))

    def step(S, inp):
        qc, kc, vc, gc = inp
        b = jnp.cumsum(gc, axis=2)
        b_last = b[:, :, -1:, :]
        qe = qc * jnp.exp(b)
        ke = kc * jnp.exp(-b)
        kd = kc * jnp.exp(b_last - b)
        att = jnp.where(mask, jnp.einsum('bhtd,bhsd->bhts', qe, ke), 0.0)
        o = jnp.einsum('bhts,bhsv->bhtv', att, vc) + jnp.einsum('bhtd,bhdv->bhtv', qe, S)
        S = jnp.exp(b_last[:, :, 0, :])[..., None] * S + jnp.einsum('bhsd,bhsv->bhdv', kd, vc)
        return S, o

    S, o = lax.scan(step, s0, (to_chunks(q), to_chunks(k), to_chunks(v), to_chunks(g)))
    o = o.transpose(1, 0, 3, 2, 4).reshape(Bn, T, H, dv)
    return o.astype(q.dtype), S

def gla_inputs(q, k, v, lr_f, lr_b, gate_w, gate_b):
    shp = q.shape[:2]
    q = q.reshape(shp + (GLA_HEADS, GLA_DK)) * GLA_DK ** -0.5
    k = k.reshape(shp + (GLA_HEADS, GLA_DK))
    v = v.reshape(shp + (GLA_HEADS, GLA_DV))

    def log_gate(lr, d):
        z = (lr @ gate_w[d] + gate_b[d]).astype(F32)
        return (jax.nn.log_sigmoid(z) / GLA_TAU).reshape(shp + (GLA_HEADS, GLA_DK))

    return q, k, v, log_gate(lr_f, 0), log_gate(lr_b, 1)

def gla_finish(o, r, g_norm):
    shp = o.shape[:2]
    return rmsnorm(o, g_norm).reshape(shp + (GLA_HEADS * GLA_DV,)) * jax.nn.silu(r)

def mla_inputs(q_dn, kv_dn, k_rope, q_g, kv_g, w_uq, w_ukv, angles):
    shp = q_dn.shape[:2]
    q = (rmsnorm(q_dn, q_g) @ w_uq).reshape(shp + (MLA_HEADS, MLA_NOPE + MLA_ROPE))
    kv = (rmsnorm(kv_dn, kv_g) @ w_ukv).reshape(shp + (MLA_HEADS, MLA_NOPE + MLA_V))
    qn, qr = q[..., :MLA_NOPE], q[..., MLA_NOPE:]
    kn, vv = kv[..., :MLA_NOPE], kv[..., MLA_NOPE:]
    if angles is not None:
        ar, ac = angles
        qr = axial_rope(qr, ar[:, None, :], ac[:, None, :])
        k_rope = axial_rope(k_rope, ar, ac)
    return qn, qr, kn, k_rope, vv

def block_attention(qn, qr, kn, kr, v):
    Bn, T, H, dn = qn.shape
    nb = T // Q_BLOCK
    scale = (MLA_NOPE + MLA_ROPE) ** -0.5
    qn_b = qn.reshape(Bn, nb, Q_BLOCK, H, dn).swapaxes(0, 1)
    qr_b = qr.reshape(Bn, nb, Q_BLOCK, H, qr.shape[-1]).swapaxes(0, 1)

    def one(args):
        qnb, qrb = args
        s = jnp.einsum('bqhd,bkhd->bhqk', qnb, kn) + jnp.einsum('bqhr,bkr->bhqk', qrb, kr)
        p = jax.nn.softmax(s.astype(F32) * scale, axis=-1).astype(v.dtype)
        return jnp.einsum('bhqk,bkhd->bqhd', p, v)

    o = lax.map(one, (qn_b, qr_b))
    return o.swapaxes(0, 1).reshape(Bn, T, H * v.shape[-1])

def merge(pool_o, gla_o, mla_o, gz, branch_w, w_out):
    shp = gz.shape[:2]
    gates = jax.nn.sigmoid(gz.astype(F32)).astype(gz.dtype).reshape(shp + (N_BRANCH, D_MODEL))
    m = (gates[..., 0, :] * (pool_o @ branch_w[0]) + gates[..., 1, :] * (gla_o @ branch_w[1])
         + gates[..., 2, :] * (mla_o @ branch_w[2]))
    return m @ w_out

def token_mixer(h, hc, w_in, pool_w, pool_scale, gate_w, gate_b, gla_g, q_g, kv_g, w_uq, w_ukv,
                branch_w, w_out, with_ctx):
    Bn, T, _ = h.shape
    angles = axial_angles(T)
    (p_in, q, k, v, r, lr_f, lr_b, q_dn, kv_dn, k_rope, gz) = split_cols(h @ w_in)
    (p_c, q_c, k_c, v_c, r_c, lr_fc, lr_bc, q_dnc, kv_dnc, k_ropec, gzc) = split_cols(hc @ w_in)

    gq, gk, gv, gf, gb = gla_inputs(q, k, v, lr_f, lr_b, gate_w, gate_b)
    cq, ck, cv, cf, cb = gla_inputs(q_c, k_c, v_c, lr_fc, lr_bc, gate_w, gate_b)
    s0 = jnp.zeros((Bn, GLA_HEADS, GLA_DK, GLA_DV), F32)
    oc_f, s_f = gla_chunk_scan(cq, ck, cv, cf, s0)
    oc_b, s_b = gla_chunk_scan(flip(cq), flip(ck), flip(cv), flip(cb), s0)
    o_f, _ = gla_chunk_scan(gq, gk, gv, gf, s_f)
    o_b, _ = gla_chunk_scan(flip(gq), flip(gk), flip(gv), flip(gb), s_b)
    gla_lat = gla_finish(o_f + flip(o_b), r, gla_g)

    qn, qr, kn, kr, vv = mla_inputs(q_dn, kv_dn, k_rope, q_g, kv_g, w_uq, w_ukv, angles)
    cqn, cqr, ckn, ckr, cvv = mla_inputs(q_dnc, kv_dnc, k_ropec, q_g, kv_g, w_uq, w_ukv, None)
    mla_lat = block_attention(qn, qr, jnp.concatenate([ckn, kn], axis=1),
                              jnp.concatenate([ckr, kr], axis=1), jnp.concatenate([cvv, vv], axis=1))

    pool_lat = multiscale_pool(p_in, pool_w, pool_scale)
    y = merge(pool_lat, gla_lat, mla_lat, gz, branch_w, w_out)
    if not with_ctx:
        return y, None
    gla_ctx = gla_finish(oc_f + flip(oc_b), r_c, gla_g)
    mla_ctx = block_attention(cqn, cqr, ckn, ckr, cvv)
    pool_ctx = multiscale_pool(p_c, pool_w, pool_scale)
    yc = merge(pool_ctx, gla_ctx, mla_ctx, gzc, branch_w, w_out)
    return y, yc

def peer(h, wq, keys, u, v):
    shp = h.shape
    xb = h.reshape(-1, PEER_BLOCK, D_MODEL)

    def one(xs):
        q = (xs @ wq).reshape(PEER_BLOCK, PEER_HEADS, 2, PEER_HALF)
        s1 = jnp.einsum('nhd,hkd->nhk', q[:, :, 0], keys[0]).astype(F32)
        s2 = jnp.einsum('nhd,hkd->nhk', q[:, :, 1], keys[1]).astype(F32)
        t1, i1 = lax.top_k(s1, PEER_TOPK)
        t2, i2 = lax.top_k(s2, PEER_TOPK)
        cand = (t1[..., :, None] + t2[..., None, :]).reshape(PEER_BLOCK, PEER_HEADS, PEER_TOPK * PEER_TOPK)
        cid = (i1[..., :, None] * PEER_N_KEYS + i2[..., None, :]).reshape(PEER_BLOCK, PEER_HEADS,
                                                                          PEER_TOPK * PEER_TOPK)
        top, j = lax.top_k(cand, PEER_TOPK)
        eid = jnp.take_along_axis(cid, j, axis=-1)
        g = jax.nn.softmax(top, axis=-1).astype(xs.dtype)
        a = jax.nn.gelu(jnp.einsum('nd,nhjd->nhj', xs, u[eid]), approximate=False)
        return jnp.einsum('nhj,nhjd->nd', g * a, v[eid])

    return lax.map(one, xb).reshape(shp)

def setup_inputs(seed: int = 0) -> dict:
    key = jax.random.key(seed)
    ks = jax.random.split(key, 32)
    L, D = DEPTH, D_MODEL

    def nrm(k, shape, s):
        return jax.random.normal(k, shape, F32) * s

    return {
        "x": nrm(ks[0], (BATCH, SEQ, D), 1.0),
        "c": nrm(ks[1], (BATCH, D), 1.0),
        "ctx": nrm(ks[2], (BATCH, CTX_LEN, D), 1.0),
        "c_ctx": nrm(ks[3], (D,), 1.0),
        "ada_w": nrm(ks[4], (L, D, 6 * D), 0.5 * D ** -0.5),
        "ada_b": nrm(ks[5], (L, 6 * D), 0.02),
        "norm1_g": 1.0 + nrm(ks[6], (L, D), 0.02),
        "norm2_g": 1.0 + nrm(ks[7], (L, D), 0.02),
        "w_in": nrm(ks[8], (L, D, IN_COLS), D ** -0.5),
        "pool_w": nrm(ks[9], (L, len(POOL_WINDOWS), POOL_GROUP, POOL_GROUP), POOL_GROUP ** -0.5),
        "pool_scale": 1.0 + nrm(ks[10], (L, POOL_WIDTH), 0.1),
        "gla_gate_w": nrm(ks[11], (L, 2, GLA_GATE_RANK, GLA_HEADS * GLA_DK), GLA_GATE_RANK ** -0.5),
        "gla_gate_b": nrm(ks[12], (L, 2, GLA_HEADS * GLA_DK), 0.1),
        "gla_norm_g": 1.0 + nrm(ks[13], (L, GLA_DV), 0.02),
        "mla_q_norm_g": 1.0 + nrm(ks[14], (L, MLA_Q_RANK), 0.02),
        "mla_kv_norm_g": 1.0 + nrm(ks[15], (L, MLA_KV_RANK), 0.02),
        "mla_w_uq": nrm(ks[16], (L, MLA_Q_RANK, MLA_HEADS * (MLA_NOPE + MLA_ROPE)), MLA_Q_RANK ** -0.5),
        "mla_w_ukv": nrm(ks[17], (L, MLA_KV_RANK, MLA_HEADS * (MLA_NOPE + MLA_V)), MLA_KV_RANK ** -0.5),
        "branch_w": nrm(ks[18], (L, N_BRANCH, BRANCH_WIDTH, D), BRANCH_WIDTH ** -0.5),
        "w_out": nrm(ks[19], (L, D, D), D ** -0.5),
        "peer_wq": nrm(ks[20], (L, D, PEER_HEADS * PEER_QDIM), D ** -0.5),
        "peer_keys": nrm(ks[21], (L, 2, PEER_HEADS, PEER_N_KEYS, PEER_HALF), PEER_HALF ** -0.5),
        "peer_u": nrm(ks[22], (L, PEER_N_EXPERTS, D), D ** -0.5),
        "peer_v": nrm(ks[23], (L, PEER_N_EXPERTS, D), 1.0),
        "final_norm_g": 1.0 + nrm(ks[24], (D,), 0.02),
    }

def reference(x, c, ctx, c_ctx, ada_w, ada_b, norm1_g, norm2_g, w_in, pool_w, pool_scale, gla_gate_w,
              gla_gate_b, gla_norm_g, mla_q_norm_g, mla_kv_norm_g, mla_w_uq, mla_w_ukv, branch_w, w_out,
              peer_wq, peer_keys, peer_u, peer_v, final_norm_g):
    x_lat, x_ctx = x, ctx
    for i in range(DEPTH):
        with_ctx = i < DEPTH - 1
        mod = jax.nn.silu(c) @ ada_w[i] + ada_b[i]
        modc = jax.nn.silu(c_ctx) @ ada_w[i] + ada_b[i]
        sh1, sc1, g1, sh2, sc2, g2 = jnp.split(mod[:, None, :], 6, axis=-1)
        csh1, csc1, cg1, csh2, csc2, cg2 = jnp.split(modc, 6)
        h = rmsnorm(x_lat, norm1_g[i]) * (1.0 + sc1) + sh1
        hc = rmsnorm(x_ctx, norm1_g[i]) * (1.0 + csc1) + csh1
        y, yc = token_mixer(h, hc, w_in[i], pool_w[i], pool_scale[i], gla_gate_w[i], gla_gate_b[i],
                            gla_norm_g[i], mla_q_norm_g[i], mla_kv_norm_g[i], mla_w_uq[i], mla_w_ukv[i],
                            branch_w[i], w_out[i], with_ctx)
        x_lat = x_lat + g1 * y
        h2 = rmsnorm(x_lat, norm2_g[i]) * (1.0 + sc2) + sh2
        x_lat = x_lat + g2 * peer(h2, peer_wq[i], peer_keys[i], peer_u[i], peer_v[i])
        if with_ctx:
            x_ctx = x_ctx + cg1 * yc
            hc2 = rmsnorm(x_ctx, norm2_g[i]) * (1.0 + csc2) + csh2
            x_ctx = x_ctx + cg2 * peer(hc2, peer_wq[i], peer_keys[i], peer_u[i], peer_v[i])
    return rmsnorm(x_lat, final_norm_g)


_drawn_inputs = setup_inputs


def setup_inputs(seed=0):
    import zlib

    import numpy as np

    out = dict(_drawn_inputs(seed))
    spreads = {}
    factors = {'gla_norm_g': 3.505, 'mla_q_norm_g': 7.115, 'mla_kv_norm_g': 5.375, 'final_norm_g': 2.854}
    for name, (base, spread) in spreads.items():
        noise = np.random.default_rng([zlib.crc32(name.encode()), seed]).standard_normal(out[name].shape)
        drawn = base * np.exp(spread * noise) if base else spread * noise
        out[name] = __import__('jax').numpy.asarray(drawn.astype(out[name].dtype))
    for name, factor in factors.items():
        out[name] = (out[name] * factor).astype(out[name].dtype)
    return out
```

```python
from contextlib import ExitStack

import numpy as np
import concourse.bass as bass
from concourse import mybir

F32 = mybir.dt.float32
U32 = mybir.dt.uint32
ALU = mybir.AluOpType
ACT = mybir.ActivationFunctionType
AX_X = mybir.AxisListType.X

P = 128
DEPTH = 2
D = 1024
DC = D // P
T_CTX, T_LAT = 256, 256
T = T_CTX + T_LAT
TILES = T // P
GRID_W = 64
EPS = 1e-6
WINDOWS = (2, 4, 8, 16)
GLA_H, DK, DV, RANK, TAU, CHUNK = 4, 128, 256, 16, 16.0, 64
MLA_H, QR, KVR, NOPE, ROPE, MV = 8, 384, 256, 128, 64, 128
ATT_SCALE = float(NOPE + ROPE) ** -0.5
PH, PK, PTOP, PHALF = 8, 128, 16, 128
N_EXP = PK * PK
SETS = 2 * PH
CAND = PTOP * PTOP
BANKS = 8
QUAD = 512
HUGE = 3.0e38

C_TRI, C_ID, C_ONE, C_DUP, C_CS, C_IOTA = 0, 256, 384, 512, 640, 1152
C_N = 1168
V_ADAB, V_N1, V_N2, V_PS, V_QG, V_KVG, V_GLA, V_L = 0, 48, 56, 64, 72, 75, 77, 79
V_FG, V_C, V_CC, V_N = DEPTH * V_L, DEPTH * V_L + DC, DEPTH * V_L + 2 * DC, DEPTH * V_L + 3 * DC
SH1, SC1, G1, SH2, SC2, G2 = range(6)

RING = 8
UNITS = PH


class Count:

    def __init__(self, known=None):
        self.known, self.table, self.total = known or {}, {}, {}
        self.sems = {}

    def mark(self, sem, *keys):
        n = self.total[sem] = self.total.get(sem, 0) + 1
        for k in keys:
            assert k not in self.table, k
            self.table[k] = (sem, n)
        return self.sems[sem], 1

    def at(self, *key):
        if not self.known:
            return next(iter(self.sems.values())), 1
        sem, n = self.known[key]
        return self.sems[sem], n


def tokens(layer):
    return (0, T) if layer < DEPTH - 1 else (T_CTX, T)


MOD_FIRST = [(0, q) for q in range(4)]
MOD_LATER = [(0, q) for q in range(4, 12)] + [(n, q) for n in range(1, DEPTH) for q in range(12)]
MOD_PLACES = ("p", "diff", "pool", "q", "k", "v", "r") + tuple("gla%d" % n for n in range(2 * TILES)) + (
    "mla2", "mla8", "mla14", "mla20", "mla26")


def mod_share(place):
    return [MOD_LATER[MOD_PLACES.index(place)]] if place in MOD_PLACES else []


def build(nc, d, cnt, banks_of, quads_of):
    mark, at = cnt.mark, cnt.at
    ctx = ExitStack()
    with ctx:
        def sb(name, shape, dt=F32):
            return ctx.enter_context(nc.sbuf_tensor(name, shape, dt))

        def sem(name):
            s = cnt.sems[name] = ctx.enter_context(nc.semaphore(name))
            return s

        const = sb("const", [P, C_N])
        vec = sb("vec", [P, V_N])
        gate_w = sb("gate_w", [RANK + 1, 2, GLA_H * DK])
        W = [sb("weights0", [P, DC * QUAD]), None]
        XT = sb("xT", [P, DC, T])
        HT = sb("hT", [P, DC, T])
        GT = sb("glaT", [P, DC, T])
        BIG = 4 * DC * T
        R = sb("region", [P, DC * T * 2 + BIG + 6144])
        W[1] = R[:, 0:DC * QUAD]
        PT = R[:, DC * T:2 * DC * T].rearrange("p (c t) -> p c t", c=DC)
        o0 = 2 * DC * T
        rg = [R[:, o0 + n * DC * T:o0 + (n + 1) * DC * T] for n in range(4)]
        A, B, C, Dr = (x.rearrange("p (c t) -> p c t", c=DC) for x in rg)
        Atok, Btok, Ctok, Dtok = (x.rearrange("p (t c) -> p t c", t=TILES) for x in rg)
        GTtok = GT[:, :, :].rearrange("p c t -> p (c t)").rearrange("p (t c) -> p t c", t=TILES)
        E = R[:, o0 + BIG:o0 + BIG + 6144]
        scr = sb("scratch", [P, 3, T])
        mods = sb("mods", [P, DEPTH, 48, 2])
        amod = sb("amod", [P, DEPTH, 2, DC, 2])
        cT = sb("cT", [P, DC, 32])
        modrow = sb("modrow", [P, P])
        small = sb("small", [P, 64])
        zeros = sb("zeros", [P, P])
        eps = small[:, 0:1]

        ps = [ctx.enter_context(nc.psum_tensor(f"bank{n}", [P, 512], F32)) for n in range(BANKS)]

        tri = const[:, C_TRI:C_TRI + 256].rearrange("p (d t) -> p d t", d=2)
        ident = const[:, C_ID:C_ID + P]
        ones = const[:, C_ONE:C_ONE + P]
        one1 = const[:, C_ONE:C_ONE + 1]
        dup = const[:, C_DUP:C_DUP + P]
        cs = const[:, C_CS:C_CS + T]
        iota16 = const[:, C_IOTA:C_IOTA + 16]

        def V(off, n, layer=0):
            return vec[:, layer * V_L + off:layer * V_L + off + n]

        def gla_buf(n, what):
            m = n % 3 * 3 + what
            x = E[:, m * 512:(m + 1) * 512] if m < 8 else scr[:, 0, :]
            return x.rearrange("p (h t) -> p h t", h=GLA_H)
        GQ, GK, GD = range(3)
        GA = GK
        state = E[:, 4096:6144].rearrange("p (d h v) -> p d h v", d=2, h=GLA_H)
        lr17 = E[0:RANK + 1, 0:1024].rearrange("p (d t) -> p d t", d=2)
        decay = sb("decay", [P, 3, GLA_H, 2])
        qd = E[:, 0:1536].rearrange("p (c t) -> p c t", c=3)
        kvd = E[:, 1536:2560].rearrange("p (c t) -> p c t", c=2)
        krope = E[:, 2560:3072]
        prob = E[:, 3072:4096].rearrange("p (n t) -> p n t", n=2)
        probT = E[:, 4096:5120].rearrange("p (n k t) -> p n k t", n=2, k=4)
        keys0 = scr[:, 1:2, :]
        pqT = R[:, o0:o0 + 2 * DC * T].rearrange("p (s t) -> p s t", s=SETS)
        S0 = o0 + 2 * DC * T
        SU = 2 * PK
        ringslot = [R[:, n * 2 * D:(n + 1) * 2 * D] for n in range(RING)]
        E2 = E[:, SU:6144]
        pos = [0]

        def e2(n):
            pos[0] += n
            return E2[:, pos[0] - n:pos[0]]
        top1 = e2(32).rearrange("p (h k) -> p h k", h=2)
        sec = e2(256).rearrange("p (h k) -> p h k", h=2)
        cand, cand2 = e2(256), e2(256)
        top, shifted, expd, rec = e2(16), e2(16), e2(32).rearrange("p (n k) -> p n k", n=2), e2(4)
        idxf, jf, chosen, onehot, eidf = e2(32), e2(32), e2(32), e2(512), e2(16)
        wts = e2(32).rearrange("p (n k) -> p n k", n=2)
        dots = e2(32).rearrange("p (n k) -> p n k", n=2)
        gel, gelw = e2(4), e2(4)
        esum = e2(2)
        unit_scores = e2(SU)
        diag = e2(512).rearrange("p (n k) -> p n k", n=4)
        topidx = sb("topidx", [P, 2, PTOP], U32)
        jidx = sb("jidx", [P, PTOP], U32)
        jparts = sb("jparts", [P, 2, PTOP], U32)
        eid = sb("eid", [P, 2, PTOP], U32)

        landed = [sem("weights0_landed"), sem("weights1_landed")]
        const_landed, x_landed, gatew_landed, keys0_landed, stored = (sem(n) for n in (
            "const_landed", "x_landed", "gatew_landed", "keys0_landed", "stored"))
        for n in ("psum_full", "evicted_by_act", "evicted_by_dve", "act_step", "dve_step", "pool_step", "dve_topk",
                  "eids_ready", "shift_ready", "exp_ready", "wts_ready", "dot_done", "act_gelu", "diag_ready",
                  "row_used", "dve_passed", "pool_passed"):
            sem(n)
        S = cnt.sems
        gathered = [sem(f"gathered{n}") for n in range(RING)]
        bank_no = {k: n % BANKS for n, k in enumerate(banks_of)}
        quad_log, bank_log = [], []
        block = ctx.enter_context(nc.Block())

        def rng(layer):
            return slice(*tokens(layer))

        def tiles(layer):
            return range(tokens(layer)[0] // P, TILES)

        def streams(layer):
            return range(tokens(layer)[0] // T_CTX, 2)

        def span(s):
            return slice(s * 256, s * 256 + 256)

        def tok(t):
            return slice(t * P, t * P + P)

        def gla_units(layer):
            fwd, bwd = [0, 1, 2, 3], [1, 0, 3, 2]
            return [u for a, b in zip(fwd, bwd) for u in ((0, a), (1, b))]

        def att_units(layer):
            return [(t, h) for t in tiles(layer) for h in range(MLA_H)]

        def peer_base(layer):
            u = sum(len(tiles(n)) * UNITS for n in range(layer))
            return u, u + layer

        @block.sync
        def _(sp):
            sp.dma_start(const[:], d["const"]).then_inc(const_landed, 16)
            sp.dma_start(vec[:], d["vec"]).then_inc(const_landed, 16)
            sp.dma_start(XT[:], d["xT"].rearrange("(c p) t -> p c t", p=P)).then_inc(x_landed, 16)
            peers = [0]
            for n, (key, src, last) in enumerate(quads_of):
                if key[1] == "p" and key[2] == 0:
                    if key[0]:
                        sp.wait_ge(*at("full", key[0] - 1, "z", 1, TILES - 1))
                    sp.dma_start(gate_w[:], d["gate"][key[0]]).then_inc(gatew_landed, 16)
                if n >= 2:
                    sp.wait_ge(*at("full", *quads_of[n - 2][2]))
                if n >= 2 and n % 2 == 1 and peers[n] > peers[n - 2]:
                    u = peer_base(peers[n])[0]
                    sp.wait_ge(S["row_used"], u * PTOP + RING)
                if key[1:] == ("wq", 2):
                    sp.wait_ge(*at("sqmm", key[0], "norm2", DC - 1))
                    sp.dma_start(keys0, d["keys"][key[0]][:, 0:4 * PK].rearrange("p (k c) -> p k c", k=1)).then_inc(
                        keys0_landed, 16)
                peers.append(peers[n] + (key[1] == "keys"))
                k, ncol = src.shape[1], src.shape[2]
                dst = W[n % 2][:, 0:k * ncol].rearrange("p (k c) -> p k c", k=k)
                sp.dma_start(dst, src).then_inc(landed[n % 2], 16)
            sp.wait_ge(*at("final", DC - 1))
            sp.dma_start(d["out"].rearrange("(c p) t -> p c t", p=P), HT[:, :, T_CTX:T]).then_inc(stored, 16)
            sp.wait_ge(stored, 16)

        @block.tensor
        def _(pe):
            cur = {}

            def quad(key, src):
                n = len(quad_log)
                quad_log.append([key, src, None])
                pe.wait_ge(landed[n % 2], 16 * (n // 2 + 1))
                cur["q"] = n
                return W[n % 2][:, 0:src.shape[1] * src.shape[2]].rearrange("p (k c) -> p k c", k=src.shape[1])

            def job(*key):
                n = len(bank_log)
                bank_log.append(key)
                if n >= BANKS:
                    pe.wait_ge(*at("evicted", *bank_log[n - BANKS]))
                if cur.get("q") is not None:
                    quad_log[cur["q"]][2] = key
                return ps[n % BANKS]

            def full(ins, *key):
                ins.then_inc(*mark("psum_full", ("full",) + key))

            def rows(ap):
                return ap.rearrange("(k p) c -> p k c", p=P)

            def mm(out, lhsT, rhs, first, last, **kw):
                return nc.tensor.matmul(out, lhsT, rhs, start=first, stop=last, **kw)

            def square_sums(name, i, n):
                b = job(i, name)
                for c in range(n):
                    pe.wait_ge(*at("sq", i, name, c))
                    r = slice(0, T) if name in ("norm1", "kvn") else rng(i)
                    x = mm(b[:, r], ones, scr[:, c % 2, r], c == 0, c == n - 1)
                    keys = [("sqmm", i, name, c)] + ([("full", i, name)] if c == n - 1 else [])
                    x.then_inc(*mark("psum_full", *keys))

            def project(i, name, w, chunks, src, nk, r, c0=0):
                for c, (off, m) in enumerate(chunks):
                    b = job(i, name, c0 + c)
                    for k in range(nk):
                        x = mm(b[0:m, r], w[:, k, off:off + m], src[:, k, r], k == 0, k == nk - 1)
                    full(x, i, name, c0 + c)

            def open_banks(i, name, keys, operands, norm):
                banks = [job(i, name, *key) for key in keys]
                for k in range(DC):
                    pe.wait_ge(*at("h", i, norm, k))
                    for n, b in enumerate(banks):
                        out, lhsT, rhs = operands(b, n, k)
                        x = mm(out, lhsT, rhs, k == 0, k == DC - 1)
                        if k == DC - 1:
                            full(x, i, name, *keys[n])

            def key_scores(i, w, t, g, wait):
                b = job(i, "ks", t, g)
                for c in range(4):
                    s = g * 4 + c
                    if wait:
                        pe.wait_ge(*at("evicted", i, "pq", s))
                    x = mm(b[:, c * P:c * P + P], pqT[:, s, tok(t)], w[:, 0, s * PK:s * PK + PK], True, True)
                full(x, i, "ks", t, g)

            def project_tokens(i, name, q, w, src, nk, tl):
                for t in tl:
                    b = job(i, name, q, t)
                    for k in range(nk):
                        x = mm(b[:, :], src[:, k, tok(t)], w[:, k, :], k == 0, k == nk - 1)
                    full(x, i, name, q, t)

            def modulate(n, q):
                w = quad((n, "mod", q), rows(d["ada_w"][n][:, q * QUAD:(q + 1) * QUAD]))
                b = job(n, "modr", q)
                for k in range(DC):
                    for c in range(4):
                        x = mm(b[32 * c:32 * c + 32, 0:P], cT[:, k, :], w[:, k, c * P:c * P + P], k == 0, k == DC - 1)
                full(x, n, "modr", q)
                cur["q"] = None

            def turn_mod(n, q):
                pe.wait_ge(*at("evicted", n, "modr", q))
                b = job(n, "mod", q)
                full(nc.tensor.transpose(b[:, 0:P], modrow[:, :], ident), n, "mod", q)

            def beside(i, place):
                if i == 0:
                    for n, q in mod_share(place):
                        modulate(n, q)
                        turn_mod(n, q)

            four = [(n * P, P) for n in range(4)]
            ALLT = slice(0, T)
            pe.wait_ge(const_landed, 32)
            pe.wait_ge(x_landed, 16)
            for i in range(DEPTH):
                r, tl, st = rng(i), tiles(i), streams(i)
                win = d["w_in"][i]
                square_sums("norm1", i, DC)
                if i == 0:
                    pe.wait_ge(*at("cT"))
                    for n, q in MOD_FIRST:
                        modulate(n, q)
                        turn_mod(n, q)
                for q in range(2):
                    w = quad((i, "p", q), rows(win[:, q * QUAD:(q + 1) * QUAD]))
                    if q == 0:
                        open_banks(i, "p", [(q, t) for t in tl],
                                   lambda b, n, k: (b[:, :], HT[:, k, tok(tl[n])], w[:, k, :]), "norm1")
                    else:
                        project_tokens(i, "p", q, w, HT, DC, tl)
                beside(i, "p")
                w = quad((i, "band"), d["band"].rearrange("p (k c) -> p k c", k=8))
                for c in range(DC):
                    if c in (0, 4):
                        for t in tl:
                            pe.wait_ge(*at("evicted", i, "p", c // 4, t))
                    b = job(i, "diff", c)
                    for s in st:
                        for k in range(2):
                            x = mm(b[:, span(s)], Atok[:, s * 2 + k, c * P:c * P + P], w[:, (c // 2) * 2 + k, :],
                                   k == 0, k == 1)
                    full(x, i, "diff", c)
                beside(i, "diff")
                w = quad((i, "pool"), d["pool_w"][i].rearrange("g (k p) c -> p (g k) c", p=P))
                for c in range(DC):
                    g = c // 2
                    if c % 2 == 0:
                        for k in range(2):
                            pe.wait_ge(*at("evicted", i, "diff", 2 * g + k))
                    b = job(i, "pool", c)
                    for k in range(2):
                        x = mm(b[:, r], w[:, g * 2 + k, (c % 2) * P:(c % 2) * P + P], B[:, 2 * g + k, r], k == 0, k == 1)
                    full(x, i, "pool", c)
                beside(i, "pool")
                w = quad((i, "lr"), rows(d["w_lr"][i]))
                project(i, "lr", w, [(0, RANK), (RANK, RANK)], HT, DC, ALLT)
                w = quad((i, "q"), rows(win[:, 1024:1536]))
                project(i, "q", w, four, HT, DC, r)
                beside(i, "q")
                w = quad((i, "k"), rows(win[:, 1536:2048]))
                project(i, "k", w, four, HT, DC, ALLT)
                beside(i, "k")
                pe.wait_ge(gatew_landed, 16 * (i + 1))
                for dd in range(2):
                    pe.wait_ge(*at("evicted", i, "lr", dd))
                    for t in range(TILES):
                        b = job(i, "z", dd, t)
                        x = mm(b[:, :], lr17[:, dd, tok(t)], gate_w[:, dd, :], True, True)
                        full(x, i, "z", dd, t)
                for q in range(2):
                    w = quad((i, "v", q), rows(win[:, 2048 + q * QUAD:2048 + (q + 1) * QUAD]))
                    project_tokens(i, "v", q, w, HT, DC, range(TILES))
                beside(i, "v")
                for q in range(2):
                    w = quad((i, "r", q), rows(win[:, 3072 + q * QUAD:3072 + (q + 1) * QUAD]))
                    project_tokens(i, "r", q, w, HT, DC, tl)
                beside(i, "r")
                cur["q"] = None
                units = gla_units(i)

                def cumulate(n):
                    dd, t = units[n]
                    pe.wait_ge(*at("gate", i, dd, t))
                    b = job(i, "b", n)
                    for h in range(GLA_H):
                        x = mm(b[:, h * P:h * P + P], Dtok_gate(dd, t)[:, h * P:h * P + P], tri[:, dd, :], True, True)
                    full(x, i, "b", n)

                def Dtok_gate(dd, t):
                    return rg[3][:, (dd * TILES + t) * 512:(dd * TILES + t + 1) * 512]

                def intra(n):
                    dd, t = units[n]
                    if t in tl:
                        pe.wait_ge(*at("gla_ke", i, n))
                        b = job(i, "att", n)
                        for h in range(GLA_H):
                            x = mm(b[:, h * P:h * P + P], gla_buf(n, GK)[:, h, :], gla_buf(n, GQ)[:, h, :], True, True)
                        full(x, i, "att", n)
                    pe.wait_ge(*at("gla_kd", i, n))
                    b = job(i, "kdt", n)
                    for h in range(GLA_H):
                        x = nc.tensor.transpose(b[:, h * P:h * P + P], gla_buf(n, GD)[:, h, :], ident)
                    full(x, i, "kdt", n)

                def outputs(n):
                    dd, t = units[n]
                    out = t in tl
                    order = (0, 1) if dd == 0 else (1, 0)
                    if out:
                        pe.wait_ge(*at("gla_att", i, n))
                        ob = [job(i, "o", n, g) for g in range(2)]
                        for h in range(GLA_H):
                            mm(ob[h // 2][:, (h % 2) * DV:(h % 2) * DV + DV], gla_buf(n, GA)[:, h, :],
                               Btok[:, t, h * DV:h * DV + DV], h % 2 == 0, False, skip_group_check=True)
                    pe.wait_ge(*at("evicted", i, "kdt", n))
                    for m, cc in enumerate(order):
                        half = slice(cc * CHUNK, cc * CHUNK + CHUNK)
                        if out:
                            if m == 0 and n >= 2:
                                pe.wait_ge(*at("evicted", i, "s", n - 2, 1, 1))
                            elif m == 0:
                                pe.wait_ge(*at("state0", i, dd))
                            else:
                                pe.wait_ge(*at("evicted", i, "s", n, 0, 1))
                            for h in range(GLA_H):
                                x = mm(ob[h // 2][half, (h % 2) * DV:(h % 2) * DV + DV], gla_buf(n, GQ)[:, h, half],
                                       state[:, dd, h, :], False, m == 1, skip_group_check=True)
                                if m == 1 and h % 2:
                                    full(x, i, "o", n, h // 2)
                        for g in range(2):
                            b = job(i, "s", n, m, g)
                            for h in (2 * g, 2 * g + 1):
                                x = mm(b[:, (h % 2) * DV:(h % 2) * DV + DV], gla_buf(n, GD)[half, h, :],
                                       Btok[half, t, h * DV:h * DV + DV], True, True)
                            full(x, i, "s", n, m, g)

                for q in range(2):
                    for t in range(TILES):
                        pe.wait_ge(*at("evicted", i, "v", q, t))
                cumulate(0)
                for n in range(len(units) + 1):
                    if n < len(units):
                        intra(n)
                    if n + 1 < len(units):
                        cumulate(n + 1)
                    if n >= 1:
                        outputs(n - 1)
                    if n < len(units):
                        beside(i, "gla%d" % n)
                for t in tl:
                    pe.wait_ge(*at("gla_fin", i, t))
                    for g in range(2):
                        b = job(i, "glat", t, g)
                        for c in range(4):
                            x = nc.tensor.transpose(b[:, c * P:c * P + P], Ctok[:, t, (g * 4 + c) * P:(g * 4 + c) * P + P],
                                                    ident)
                        full(x, i, "glat", t, g)
                w = quad((i, "qk"), rows(d["w_qk"][i]))
                project(i, "qd", w, four[:3], HT, DC, r)
                project(i, "kr", w, four[3:], HT, DC, ALLT)
                w = quad((i, "kv"), rows(d["w_kv"][i]))
                project(i, "kvd", w, four[:2], HT, DC, ALLT)
                cur["q"] = None
                square_sums("qn_", i, 3)
                square_sums("kvn", i, 2)
                pe.wait_ge(*at("evicted", i, "kr", 0))
                b = job(i, "krd")
                x = mm(b[:, :], dup, krope, True, True)
                full(x, i, "krd")
                for q in range(2):
                    w = quad((i, "uqn", q), rows(d["w_uqn"][i][:, q * QUAD:(q + 1) * QUAD]))
                    pe.wait_ge(*at("qn", i, 2))
                    project(i, "qn", w, four, qd, 3, r, 4 * q)
                for q in range(2):
                    w = quad((i, "uqr", q), rows(d["w_uqr"][i][:, q * QUAD:(q + 1) * QUAD]))
                    project(i, "qr", w, four, qd, 3, r, 4 * q)
                for q in range(2):
                    w = quad((i, "ukn", q), rows(d["w_ukn"][i][:, q * QUAD:(q + 1) * QUAD]))
                    pe.wait_ge(*at("kvn_", i, 1))
                    project(i, "kn", w, four, kvd, 2, ALLT, 4 * q)
                for q in range(2):
                    w = quad((i, "ukv", q), rows(d["w_ukv"][i][:, q * QUAD:(q + 1) * QUAD]))
                    project_tokens(i, "vv", q, w, kvd, 2, range(TILES))
                cur["q"] = None
                au = att_units(i)

                def scores(n):
                    t, h = au[n]
                    nk = (2 if t < 2 else 4) * P
                    if t == au[0][0]:
                        for name in ("qn", "qr", "kn"):
                            pe.wait_ge(*at("evicted", i, name, h))
                    b = job(i, "sc", n)
                    mm(b[:, 0:nk], A[:, h, tok(t)], C[:, h, 0:nk], True, False)
                    x = mm(b[:, 0:nk], B[:, h, tok(t)], krope[:, 0:nk], False, True)
                    full(x, i, "sc", n)

                def turn(n):
                    t, h = au[n]
                    pe.wait_ge(*at("prob", i, n))
                    b = job(i, "pt", n)
                    for k in range(2 if t < 2 else 4):
                        x = nc.tensor.transpose(b[:, k * P:k * P + P], prob[:, n % 2, k * P:k * P + P], ident)
                    full(x, i, "pt", n)

                def weigh(n):
                    t, h = au[n]
                    nk = 2 if t < 2 else 4
                    pe.wait_ge(*at("evicted", i, "pt", n))
                    b = job(i, "ao", n)
                    for k in range(nk):
                        x = mm(b[:, 0:P], Dtok[:, k, h * MV:h * MV + MV], probT[:, n % 2, k, :], k == 0, k == nk - 1)
                    full(x, i, "ao", n)

                pe.wait_ge(*at("evicted", i, "krd"))
                for q in range(2):
                    for t in range(TILES):
                        pe.wait_ge(*at("evicted", i, "vv", q, t))
                scores(0)
                scores(1)
                for n in range(len(au) + 1):
                    if n + 2 < len(au):
                        scores(n + 2)
                    later = mod_share("mla%d" % n) if i == 0 else []
                    for m in later:
                        modulate(*m)
                    if n < len(au):
                        turn(n)
                    for m in later:
                        turn_mod(*m)
                    if n >= 1:
                        weigh(n - 1)
                for cq in range(2):
                    for br, src in enumerate((PT, GT, A)):
                        w = quad((i, "gz", cq, br), rows(win[:, 4832 + br * D + cq * QUAD:4832 + br * D + (cq + 1) * QUAD]))
                        project(i, "gz%d" % br, w, four, HT, DC, r, 4 * cq)
                        w = quad((i, "bw", cq, br), rows(d["branch_w"][i, br][:, cq * QUAD:(cq + 1) * QUAD]))
                        if cq == 0 and br == 0:
                            for c in range(DC):
                                pe.wait_ge(*at("evicted", i, "pool", c))
                        if cq == 0 and br == 1:
                            for t in tl:
                                for g in range(2):
                                    pe.wait_ge(*at("evicted", i, "glat", t, g))
                        if cq == 0 and br == 2:
                            pe.wait_ge(*at("evicted", i, "ao", len(au) - 1))
                        project(i, "bw%d" % br, w, four, src, DC, r, 4 * cq)
                for q in range(2):
                    w = quad((i, "wo", q), rows(d["w_out"][i][:, q * QUAD:(q + 1) * QUAD]))
                    for c in range(DC):
                        pe.wait_ge(*at("evicted", i, "bw2", c))
                    project(i, "y", w, four, B, DC, r, 4 * q)
                cur["q"] = None
                square_sums("norm2", i, DC)
                for q in range(4):
                    w = quad((i, "wq", q), rows(d["peer_wq"][i][:, q * QUAD:(q + 1) * QUAD]))
                    if q == 0:
                        open_banks(i, "pq", [(c,) for c in range(4)],
                                   lambda b, n, k: (b[:, r], w[:, k, n * P:n * P + P], HT[:, k, r]), "norm2")
                    else:
                        project(i, "pq", w, four, HT, DC, r, 4 * q)
                    if q == 1:
                        pe.wait_ge(keys0_landed, 16 * (i + 1))
                        key_scores(i, keys0, tl[0], 0, True)
                cur["q"] = None
                for t in tl:
                    for g in range(2):
                        b = job(i, "ht", t, g)
                        for c in range(4):
                            x = nc.tensor.transpose(b[:, c * P:c * P + P], HT[:, g * 4 + c, tok(t)], ident)
                        full(x, i, "ht", t, g)
                w = quad((i, "keys"), d["keys"][i].rearrange("p (k c) -> p k c", k=1))
                for t in tl:
                    for g in range(4):
                        if (t, g) != (tl[0], 0):
                            key_scores(i, w, t, g, t == tl[0])
                cur["q"] = None
                u0, _ = peer_base(i)
                for lt, t in enumerate(tl):
                    acc = [job(i, "acc", t, g) for g in range(2)]
                    for g in range(2):
                        mm(acc[g][:, :], zeros[:, :], cs, True, False, skip_group_check=True)
                    with pe.Fori(0, UNITS // 2) as it:
                        for par in range(2):
                            for j in range(PTOP):
                                J = (u0 + lt * UNITS + par) * PTOP + j
                                pe.wait_ge(S["diag_ready"], it * (2 * PTOP) + J + 1)
                                for g in range(2):
                                    x = mm(acc[g][:, :], diag[:, j % 4, :],
                                           ringslot[j % RING][:, D + g * 512:D + g * 512 + 512], False, False,
                                           skip_group_check=True)
                                x.then_inc(S["row_used"], 1)
                    for g in range(2):
                        pe.wait_ge(*at("evicted", i, "acc", t, g))
                        b = job(i, "yt", t, g)
                        for c in range(4):
                            x = nc.tensor.transpose(b[:, c * P:c * P + P], GTtok[:, t, (g * 4 + c) * P:(g * 4 + c) * P + P],
                                                    ident)
                        full(x, i, "yt", t, g)
            square_sums("normf", DEPTH - 1, DC)

        banks_of[:] = bank_log
        quads_of[:] = quad_log

        def bank(eng, *key):
            eng.wait_ge(*at("full", *key))
            return ps[bank_no.get(key, 0)]

        ACT_EV = "evicted_by_act"
        DVE_EV = "evicted_by_dve"

        @block.scalar
        def _(act):
            def copy_out(out, b, *key, scale=None):
                x = nc.scalar.activation(out, b, ACT.Copy, scale=1.0 if scale is None else scale)
                x.then_inc(*mark(ACT_EV, ("evicted",) + key))

            def squares(name, i, n, src, r):
                for c in range(n):
                    if c >= 2:
                        act.wait_ge(*at("sqmm", i, name, c - 2))
                    nc.scalar.activation(scr[:, c % 2, r], src[:, c, r], ACT.Square).then_inc(
                        *mark("act_step", ("sq", i, name, c)))

            def root(name, i, width, r):
                b = bank(act, i, name)
                nc.scalar.activation(scr[:, 2, r], b[:, r], ACT.Sqrt, bias=eps, scale=1.0 / width).then_inc(
                    *mark(ACT_EV, ("evicted", i, name)))

            def shift(name, i, sh):
                for c in range(DC):
                    act.wait_ge(*at("scaled", i, name, c))
                    for s in streams(i):
                        x = nc.scalar.activation(HT[:, c, span(s)], HT[:, c, span(s)], ACT.Identity,
                                                 bias=mods[:, i, sh * DC + c, s:s + 1])
                    x.then_inc(*mark("act_step", ("h", i, name, c)))

            act.wait_ge(const_landed, 32)
            act.wait_ge(*at("eps"))
            act.wait_ge(*at("cT0"))
            nc.scalar.activation(cT[:, :, 1], vec[:, V_C:V_C + DC], ACT.Silu)
            nc.scalar.activation(cT[:, :, 0], vec[:, V_CC:V_CC + DC], ACT.Silu).then_inc(*mark("act_step", ("cT",)))
            act.wait_ge(x_landed, 16)

            def row_out(n, q):
                b = bank(act, n, "modr", q)
                copy_out(modrow[:, :], b[:, 0:P], n, "modr", q)

            def beside(i, place):
                if i == 0:
                    for n, q in mod_share(place):
                        row_out(n, q)

            for i in range(DEPTH):
                r, tl, st = rng(i), tiles(i), streams(i)
                ALLT = slice(0, T)
                if i:
                    act.wait_ge(*at("x2", i - 1, DC - 1))
                for c in range(DC):
                    if c >= 2:
                        act.wait_ge(*at("sqmm", i, "norm1", c - 2))
                    nc.scalar.activation(scr[:, c % 2, ALLT], XT[:, c, ALLT], ACT.Square).then_inc(
                        *mark("act_step", ("sq", i, "norm1", c)))
                root("norm1", i, D, ALLT)
                if i == 0:
                    for n, q in MOD_FIRST:
                        row_out(n, q)
                for c in range(DC):
                    act.wait_ge(*at("scaled", i, "norm1", c))
                    for s in range(2):
                        x = nc.scalar.activation(HT[:, c, span(s)], HT[:, c, span(s)], ACT.Identity,
                                                 bias=mods[:, i, SH1 * DC + c, s:s + 1])
                    x.then_inc(*mark("act_step", ("h", i, "norm1", c)))
                for q in range(2):
                    for t in tl:
                        if t % 2:
                            b = bank(act, i, "p", q, t)
                            copy_out(Atok[:, t, q * QUAD:(q + 1) * QUAD], b[:, :], i, "p", q, t)
                beside(i, "p")
                for c in range(1, DC, 2):
                    b = bank(act, i, "diff", c)
                    copy_out(B[:, c, r], b[:, r], i, "diff", c)
                beside(i, "diff")
                for c in range(DC):
                    b = bank(act, i, "pool", c)
                    copy_out(PT[:, c, r], b[:, r], i, "pool", c, scale=V(V_PS + c, 1, i))
                beside(i, "pool")
                for h in range(GLA_H):
                    b = bank(act, i, "q", h)
                    copy_out(A[:, h, r], b[:, r], i, "q", h, scale=float(DK) ** -0.5)
                beside(i, "q")
                beside(i, "k")
                for dd in range(2):
                    for t in range(TILES):
                        n = dd * TILES + t
                        if n >= 3:
                            act.wait_ge(*at("gate", i, (n - 3) // TILES, (n - 3) % TILES))
                        b = bank(act, i, "z", dd, t)
                        nc.scalar.activation(scr[:, n % 3, :], b[:, :], ACT.Abs).then_inc(
                            *mark("act_step", ("abs", i, n)))
                        act.wait_ge(*at("abs", i, n))
                        nc.scalar.activation(scr[:, n % 3, :], scr[:, n % 3, :], ACT.Exp, scale=-1.0).then_inc(
                            *mark("act_step", ("exp", i, n)))
                        act.wait_ge(*at("exp", i, n))
                        nc.scalar.activation(scr[:, n % 3, :], scr[:, n % 3, :], ACT.Ln, bias=one1).then_inc(
                            *mark("act_step", ("softplus", i, n)))
                for q in range(2):
                    for t in range(TILES):
                        if t % 2:
                            b = bank(act, i, "v", q, t)
                            copy_out(Btok[:, t, q * QUAD:(q + 1) * QUAD], b[:, :], i, "v", q, t)
                beside(i, "v")
                for q in range(2):
                    for t in tl:
                        b = bank(act, i, "r", q, t)
                        nc.scalar.activation(Ctok[:, t, q * QUAD:(q + 1) * QUAD], b[:, :], ACT.Silu).then_inc(
                            *mark(ACT_EV, ("evicted", i, "r", q, t)))
                beside(i, "r")
                units = gla_units(i)

                def decays(n):
                    dd, t = units[n]
                    if n >= 3:
                        act.wait_ge(*at("full", i, "s", n - 3, 1, 1))
                    b = bank(act, i, "b", n)
                    bv = b[:, :].rearrange("p (h t) -> p h t", h=GLA_H)
                    nc.scalar.activation(gla_buf(n, GQ), bv, ACT.Exp, scale=1.0 / TAU).then_inc(
                        *mark("act_step", ("eb", i, n)))
                    nc.scalar.activation(gla_buf(n, GK), bv, ACT.Exp, scale=-1.0 / TAU).then_inc(
                        *mark("act_step", ("enb", i, n)))
                    act.wait_ge(*at("bdiff", i, n))
                    nc.scalar.activation(gla_buf(n, GD), gla_buf(n, GD), ACT.Exp, scale=1.0 / TAU).then_inc(
                        *mark("act_step", ("ekd", i, n)))

                def keys_out(n):
                    dd, t = units[n]
                    b = bank(act, i, "kdt", n)
                    copy_out(gla_buf(n, GD), b[:, :].rearrange("p (h t) -> p h t", h=GLA_H), i, "kdt", n)

                decays(0)
                for n in range(len(units)):
                    if n + 1 < len(units):
                        decays(n + 1)
                    keys_out(n)
                    beside(i, "gla%d" % n)
                for t in tl:
                    act.wait_ge(*at("o_sum", i, t))
                    for h in range(GLA_H):
                        x = nc.scalar.activation(scr[:, 0, 0:DV], GTtok[:, t, h * DV:h * DV + DV], ACT.Square,
                                                 accum_out=small[:, 4 + h:5 + h])
                        x.then_inc(*mark("act_step", ("gsq", i, t, h)))
                        act.wait_ge(*at("gsq", i, t, h))
                    if t > tl[0]:
                        act.wait_ge(*at("gla_fin", i, t - 1))
                    nc.scalar.activation(small[:, 8:12], small[:, 4:8], ACT.Sqrt, bias=eps, scale=1.0 / DV).then_inc(
                        *mark("act_step", ("gsqrt", i, t)))
                    act.wait_ge(*at("gsqrt", i, t))
                act.wait_ge(*at("gla_fin", i, tl[-1]))
                for t in tl:
                    for g in range(2):
                        b = bank(act, i, "glat", t, g)
                        bv = b[:, :].rearrange("p (c t) -> p c t", c=4)
                        for m in range(2):
                            x = nc.scalar.activation(GT[:, g * 4 + m:g * 4 + m + 3:2, tok(t)], bv[:, m:m + 3:2, :], ACT.Copy,
                                                     scale=V(V_GLA + m, 1, i))
                        x.then_inc(*mark(ACT_EV, ("evicted", i, "glat", t, g)))
                for c in range(3):
                    b = bank(act, i, "qd", c)
                    copy_out(qd[:, c, r], b[:, r], i, "qd", c)
                for c in range(2):
                    b = bank(act, i, "kvd", c)
                    copy_out(kvd[:, c, :], b[:, :], i, "kvd", c)
                act.wait_ge(*at("evicted", i, "qd", 2))
                squares("qn_", i, 3, qd, r)
                root("qn_", i, QR, r)
                act.wait_ge(*at("evicted", i, "kvd", 1))
                squares("kvn", i, 2, kvd, ALLT)
                act.wait_ge(*at("qn", i, 2))
                root("kvn", i, KVR, ALLT)
                b = bank(act, i, "krd")
                copy_out(krope, b[:, :], i, "krd")
                for h in range(MLA_H):
                    b = bank(act, i, "qn", h)
                    copy_out(A[:, h, r], b[:, r], i, "qn", h)
                for h in range(MLA_H):
                    if h % 2:
                        b = bank(act, i, "kn", h)
                        copy_out(C[:, h, :], b[:, :], i, "kn", h)
                for q in range(2):
                    for t in range(TILES):
                        if t % 2:
                            b = bank(act, i, "vv", q, t)
                            copy_out(Dtok[:, t, q * QUAD:(q + 1) * QUAD], b[:, :], i, "vv", q, t)
                au = att_units(i)

                def expo(n):
                    t, h = au[n]
                    nk = (2 if t < 2 else 4) * P
                    act.wait_ge(*at("negmax", i, n))
                    if n >= 2:
                        act.wait_ge(*at("full", i, "pt", n - 2))
                    b = ps[bank_no.get((i, "sc", n), 0)]
                    nc.scalar.activation(prob[:, n % 2, 0:nk], b[:, 0:nk], ACT.Exp, bias=small[:, 16 + n % 2:17 + n % 2],
                                         scale=ATT_SCALE, accum_out=small[:, 20 + n % 2:21 + n % 2]).then_inc(
                        *mark(ACT_EV, ("evicted", i, "sc", n)))

                def turned(n):
                    t, h = au[n]
                    nk = 2 if t < 2 else 4
                    b = bank(act, i, "pt", n)
                    if n >= 2:
                        act.wait_ge(*at("full", i, "ao", n - 2))
                    copy_out(probT[:, n % 2, 0:nk, :], b[:, 0:nk * P].rearrange("p (k t) -> p k t", k=nk), i, "pt", n)

                expo(0)
                for n in range(len(au)):
                    if n + 1 < len(au):
                        expo(n + 1)
                    beside(i, "mla%d" % n)
                    turned(n)
                m = 0
                for cq in range(2):
                    for br in range(3):
                        for c in range(4):
                            b = bank(act, i, "gz%d" % br, cq * 4 + c)
                            if m >= 8:
                                pm = m - 8
                                act.wait_ge(*at("gated", i, pm))
                            nc.scalar.activation(C[:, m % 8, r], b[:, r], ACT.Sigmoid).then_inc(
                                *mark(ACT_EV, ("evicted", i, "gz%d" % br, cq * 4 + c)))
                            m += 1
                act.wait_ge(*at("x1", i, DC - 1))
                squares("norm2", i, DC, XT, r)
                root("norm2", i, D, r)
                shift("norm2", i, SH2)
                for s in list(range(1, 8, 2)) + list(range(8, SETS)):
                    b = bank(act, i, "pq", s)
                    copy_out(pqT[:, s, r], b[:, r], i, "pq", s)
                u0, q0 = peer_base(i)

                def softmax_exp(q, par):
                    act.wait_ge(S["shift_ready"], q + 1)
                    nc.scalar.activation(expd[:, par, :], shifted, ACT.Exp, accum_out=esum[:, par:par + 1]).then_inc(
                        S["exp_ready"], 1)

                softmax_exp(q0, 0)
                for t in tl:
                    b = bank(act, i, "ht", t, 1)
                    copy_out(GTtok[:, t, 512:1024], b[:, :], i, "ht", t, 1)
                for lt, t in enumerate(tl):
                    for g in range(1, 4, 2):
                        b = bank(act, i, "ks", t, g)
                        copy_out(R[:, S0 + lt * UNITS * SU + g * 512:S0 + lt * UNITS * SU + g * 512 + 512], b[:, :],
                                 i, "ks", t, g)
                for lt, t in enumerate(tl):
                    with act.Fori(0, UNITS // 2) as it:
                        for par in range(2):
                            u = lt * UNITS + par
                            act.wait_ge(S["wts_ready"], it * 2 + (q0 + u + 1))
                            for j in range(PTOP):
                                J0 = (u0 + u) * PTOP + j
                                act.wait_ge(S["dot_done"], it * (2 * PTOP) + (J0 + 1))
                                nc.scalar.activation(gel[:, j % 4:j % 4 + 1], dots[:, par, j:j + 1], ACT.Gelu).then_inc(
                                    S["act_gelu"], 1)
                                act.wait_ge(S["act_gelu"], it * (4 * PTOP) + (2 * J0 + 1))
                                nc.scalar.activation(gelw[:, j % 4:j % 4 + 1], gel[:, j % 4:j % 4 + 1], ACT.Copy,
                                                     scale=wts[:, par, j:j + 1]).then_inc(S["act_gelu"], 1)
                                act.wait_ge(S["act_gelu"], it * (4 * PTOP) + (2 * J0 + 2))
                                act.wait_ge(S["row_used"], it * (2 * PTOP) + (J0 + 1 - 4 + RING))
                                nc.scalar.activation(diag[:, j % 4, :], ident, ACT.Copy,
                                                     scale=gelw[:, j % 4:j % 4 + 1]).then_inc(S["diag_ready"], 1)
                                if j == PTOP // 2 - 1:
                                    softmax_exp(it * 2 + (q0 + u + 1), 1 - par)
                    act.wait_ge(S["row_used"], (u0 + (lt + 1) * UNITS) * PTOP + RING)
                    copy_out(GTtok[:, t, 512:1024], ps[bank_no.get((i, "acc", t, 1), 0)][:, :], i, "acc", t, 1)
            act.wait_ge(*at("x2", DEPTH - 1, DC - 1))
            squares("normf", DEPTH - 1, DC, XT, rng(DEPTH - 1))
            root("normf", DEPTH - 1, D, rng(DEPTH - 1))

        @block.vector
        def _(dve):
            v = nc.vector

            def copy_out(out, b, *key):
                v.tensor_copy(out, b).then_inc(*mark(DVE_EV, ("evicted",) + key))

            def inverse(name, i, r):
                dve.wait_ge(*at("evicted", i, name))
                v.reciprocal(scr[:, 2, r], scr[:, 2, r]).then_inc(*mark("dve_step", ("rstd", i, name)))
                dve.wait_ge(*at("rstd", i, name))

            v.memset(eps, EPS).then_inc(*mark("dve_step", ("eps",)))
            v.memset(cT[:, :, :], 0.0).then_inc(*mark("dve_step", ("cT0",)))
            v.memset(zeros[:, :], 0.0).then_inc(*mark("dve_step", ("zeros",)))
            dve.wait_ge(const_landed, 32)
            dve.wait_ge(x_landed, 16)

            def mod_out(n, q):
                b = bank(dve, n, "mod", q)
                v.tensor_tensor(mods[:, n, q * 4:q * 4 + 4, :],
                                b[:, 0:P].rearrange("p (c s) -> p c s", s=32)[:, :, 0:2],
                                V(V_ADAB + q * 4, 4, n).unsqueeze(2).to_broadcast([P, 4, 2]), ALU.add).then_inc(
                    *mark(DVE_EV, ("evicted", n, "mod", q)))
                for m, (sc, vg) in enumerate(((SC1, V_N1), (SC2, V_N2))):
                    if q == 2 * sc + 1:
                        dve.wait_ge(*at("evicted", n, "mod", q))
                        v.scalar_tensor_tensor(out=amod[:, n, m, :, :], in0=mods[:, n, sc * DC:sc * DC + DC, :], scalar=1.0,
                                               in1=V(vg, DC, n).unsqueeze(2).to_broadcast([P, DC, 2]),
                                               op0=ALU.add, op1=ALU.mult).then_inc(*mark("dve_step", ("amod", n, m)))

            def beside(i, place):
                if i == 0:
                    for n, q in mod_share(place):
                        mod_out(n, q)

            for i in range(DEPTH):
                r, tl, st = rng(i), tiles(i), streams(i)
                ALLT = slice(0, T)
                def scale_rows(name, m, sts):
                    for c in range(DC):
                        for s in sts:
                            x = v.scalar_tensor_tensor(out=HT[:, c, span(s)], in0=XT[:, c, span(s)],
                                                       scalar=amod[:, i, m, c, s:s + 1], in1=scr[:, 2, span(s)],
                                                       op0=ALU.mult, op1=ALU.mult)
                        x.then_inc(*mark("dve_step", ("scaled", i, name, c)))

                inverse("norm1", i, ALLT)
                if i == 0:
                    for n, q in MOD_FIRST:
                        mod_out(n, q)
                dve.wait_ge(*at("amod", i, 0))
                scale_rows("norm1", 0, range(2))
                for q in range(2):
                    for t in tl:
                        if t % 2 == 0:
                            b = bank(dve, i, "p", q, t)
                            copy_out(Atok[:, t, q * QUAD:(q + 1) * QUAD], b[:, :], i, "p", q, t)
                beside(i, "p")
                for c in range(0, DC, 2):
                    b = bank(dve, i, "diff", c)
                    copy_out(B[:, c, r], b[:, r], i, "diff", c)
                beside(i, "diff")
                beside(i, "pool")
                v.memset(lr17, 1.0).then_inc(*mark("dve_step", ("lr1", i)))
                dve.wait_ge(*at("lr1", i))
                for dd in range(2):
                    b = bank(dve, i, "lr", dd)
                    copy_out(lr17[0:RANK, dd, :], b[0:RANK, :], i, "lr", dd)
                beside(i, "q")
                for h in range(GLA_H):
                    b = bank(dve, i, "k", h)
                    copy_out(A[:, 4 + h, :], b[:, :], i, "k", h)
                beside(i, "k")
                for dd in range(2):
                    for t in range(TILES):
                        n = dd * TILES + t
                        dve.wait_ge(*at("softplus", i, n))
                        b = ps[bank_no.get((i, "z", dd, t), 0)]
                        v.scalar_tensor_tensor(out=rg[3][:, n * 512:(n + 1) * 512], in0=b[:, :], scalar=0.0,
                                               in1=scr[:, n % 3, :], op0=ALU.min, op1=ALU.subtract).then_inc(
                            *mark(DVE_EV, ("evicted", i, "z", dd, t), ("gate", i, dd, t)))
                for q in range(2):
                    for t in range(0, TILES, 2):
                        b = bank(dve, i, "v", q, t)
                        copy_out(Btok[:, t, q * QUAD:(q + 1) * QUAD], b[:, :], i, "v", q, t)
                beside(i, "v")
                beside(i, "r")
                units = gla_units(i)
                for dd in range(2):
                    v.memset(state[:, dd, :, :], 0.0).then_inc(*mark("dve_step", ("state0", i, dd)))
                dve.wait_ge(*at("evicted", i, "q", GLA_H - 1))
                dve.wait_ge(*at("evicted", i, "k", GLA_H - 1))

                def scale_keys(n):
                    dd, t = units[n]
                    b = bank(dve, i, "b", n)
                    dve.wait_ge(*at("enb", i, n))
                    blocks = b[:, :].rearrange("p (n t) -> p n t", t=CHUNK)
                    last = CHUNK - 1 if dd == 0 else 0
                    flat = gla_buf(n, GD).rearrange("p h t -> p (h t)").rearrange("p (n t) -> p n t", t=CHUNK)
                    v.tensor_copy(flat[:, :, 0:CHUNK], blocks[:, :, last:last + 1].to_broadcast([P, 8, CHUNK])).then_inc(
                        *mark("dve_step", ("blast", i, n)))
                    dve.wait_ge(*at("blast", i, n))
                    v.tensor_tensor(flat, flat, blocks, ALU.subtract).then_inc(*mark("dve_step", ("bdiff", i, n)))
                    ebf = gla_buf(n, GQ).rearrange("p h t -> p (h t)").rearrange("p (n t) -> p n t", t=CHUNK)
                    v.tensor_copy(decay[:, n % 3, :, :].rearrange("p h c -> p (h c)"), ebf[:, :, last]).then_inc(
                        *mark(DVE_EV, ("evicted", i, "b", n)))
                    dve.wait_ge(*at("evicted", i, "b", n))
                    if t in tl:
                        v.tensor_tensor(gla_buf(n, GQ), gla_buf(n, GQ), A[:, 0:4, tok(t)], ALU.mult)
                        v.tensor_tensor(gla_buf(n, GK), gla_buf(n, GK), A[:, 4:8, tok(t)], ALU.mult).then_inc(
                            *mark("dve_step", ("gla_ke", i, n)))

                def mask(n):
                    dd, t = units[n]
                    if t not in tl:
                        return
                    b = bank(dve, i, "att", n)
                    ga = gla_buf(n, GA)
                    v.tensor_scalar(ga, b[:, :].rearrange("p (h t) -> p h t", h=GLA_H), HUGE, -HUGE, ALU.min,
                                    ALU.max).then_inc(*mark(DVE_EV, ("evicted", i, "att", n)))
                    dve.wait_ge(*at("evicted", i, "att", n))
                    v.tensor_tensor(ga, ga, tri[:, dd, :].unsqueeze(1).to_broadcast([P, GLA_H, P]), ALU.mult).then_inc(
                        *mark("dve_step", ("gla_att", i, n)))

                seen = set()

                def carry(n):
                    dd, t = units[n]
                    order = (0, 1) if dd == 0 else (1, 0)
                    for m, cc in enumerate(order):
                        if m == 0 and n < 2:
                            dve.wait_ge(*at("state0", i, dd))
                        elif m == 0:
                            dve.wait_ge(*at("evicted", i, "s", n - 2, 1, 1))
                        else:
                            dve.wait_ge(*at("evicted", i, "s", n, 0, 1))
                        for g in range(2):
                            b = bank(dve, i, "s", n, m, g)
                            for h in (2 * g, 2 * g + 1):
                                x = v.scalar_tensor_tensor(out=state[:, dd, h, :], in0=state[:, dd, h, :],
                                                           scalar=decay[:, n % 3, h, cc:cc + 1],
                                                           in1=b[:, (h % 2) * DV:(h % 2) * DV + DV],
                                                           op0=ALU.mult, op1=ALU.add)
                            x.then_inc(*mark(DVE_EV, ("evicted", i, "s", n, m, g)))
                    if t in tl:
                        for g in range(2):
                            b = bank(dve, i, "o", n, g)
                            o = GTtok[:, t, g * 512:g * 512 + 512]
                            keys = [("evicted", i, "o", n, g)]
                            if t in seen:
                                if g:
                                    keys.append(("o_sum", i, t))
                                else:
                                    dve.wait_ge(*at("o_first", i, t))
                                v.tensor_tensor(o, o, b[:, :], ALU.add).then_inc(*mark(DVE_EV, *keys))
                            else:
                                if g:
                                    keys.append(("o_first", i, t))
                                v.tensor_copy(o, b[:, :]).then_inc(*mark(DVE_EV, *keys))
                        seen.add(t)

                scale_keys(0)
                for n in range(len(units) + 1):
                    if n < len(units):
                        mask(n)
                    if n + 1 < len(units):
                        scale_keys(n + 1)
                    if n >= 1:
                        carry(n - 1)
                    if n < len(units):
                        beside(i, "gla%d" % n)
                for t in tl:
                    dve.wait_ge(*at("gsqrt", i, t))
                    v.reciprocal(small[:, 12:16], small[:, 8:12]).then_inc(*mark("dve_step", ("grec", i, t)))
                    dve.wait_ge(*at("grec", i, t))
                    for q in range(2):
                        dve.wait_ge(*at("evicted", i, "r", q, t))
                    for h in range(GLA_H):
                        hv = slice(h * DV, h * DV + DV)
                        x = v.scalar_tensor_tensor(out=Ctok[:, t, hv], in0=GTtok[:, t, hv], scalar=small[:, 12 + h:13 + h],
                                                   in1=Ctok[:, t, hv], op0=ALU.mult, op1=ALU.mult)
                    x.then_inc(*mark("dve_step", ("gla_fin", i, t)))
                b = bank(dve, i, "kr", 0)
                v.tensor_tensor(krope, b[:, :], cs, ALU.mult).then_inc(*mark(DVE_EV, ("evicted", i, "kr", 0)))
                inverse("qn_", i, r)
                for c in range(3):
                    v.scalar_tensor_tensor(out=qd[:, c, r], in0=qd[:, c, r], scalar=V(V_QG + c, 1, i), in1=scr[:, 2, r],
                                           op0=ALU.mult, op1=ALU.mult).then_inc(*mark("dve_step", ("qn", i, c)))
                inverse("kvn", i, ALLT)
                for c in range(2):
                    v.scalar_tensor_tensor(out=kvd[:, c, :], in0=kvd[:, c, :], scalar=V(V_KVG + c, 1, i), in1=scr[:, 2, :],
                                           op0=ALU.mult, op1=ALU.mult).then_inc(*mark("dve_step", ("kvn_", i, c)))
                for h in range(MLA_H):
                    b = bank(dve, i, "qr", h)
                    v.tensor_tensor(B[:, h, r], b[:, r], cs[:, r], ALU.mult).then_inc(
                        *mark(DVE_EV, ("evicted", i, "qr", h)))
                for h in range(0, MLA_H, 2):
                    b = bank(dve, i, "kn", h)
                    copy_out(C[:, h, :], b[:, :], i, "kn", h)
                for q in range(2):
                    for t in range(0, TILES, 2):
                        b = bank(dve, i, "vv", q, t)
                        copy_out(Dtok[:, t, q * QUAD:(q + 1) * QUAD], b[:, :], i, "vv", q, t)
                au = att_units(i)

                def maxima(n):
                    t, h = au[n]
                    nk = (2 if t < 2 else 4) * P
                    b = bank(dve, i, "sc", n)
                    v.tensor_reduce(small[:, 18 + n % 2:19 + n % 2], b[:, 0:nk], AX_X, ALU.max).then_inc(
                        *mark("dve_step", ("max", i, n)))
                    dve.wait_ge(*at("max", i, n))
                    if n >= 2:
                        dve.wait_ge(*at("evicted", i, "sc", n - 2))
                    v.tensor_scalar(small[:, 16 + n % 2:17 + n % 2], small[:, 18 + n % 2:19 + n % 2], -ATT_SCALE, None,
                                    ALU.mult).then_inc(*mark("dve_step", ("negmax", i, n)))

                def normal(n):
                    t, h = au[n]
                    nk = (2 if t < 2 else 4) * P
                    dve.wait_ge(*at("evicted", i, "sc", n))
                    v.reciprocal(small[:, 22 + n % 2:23 + n % 2], small[:, 20 + n % 2:21 + n % 2]).then_inc(
                        *mark("dve_step", ("psum", i, n)))
                    dve.wait_ge(*at("psum", i, n))
                    v.tensor_scalar(prob[:, n % 2, 0:nk], prob[:, n % 2, 0:nk], small[:, 22 + n % 2:23 + n % 2], None,
                                    ALU.mult).then_inc(*mark("dve_step", ("prob", i, n)))

                def att_out(n):
                    t, h = au[n]
                    b = bank(dve, i, "ao", n)
                    copy_out(A[:, h, tok(t)], b[:, 0:P], i, "ao", n)

                maxima(0)
                for n in range(len(au) + 1):
                    if n < len(au):
                        normal(n)
                    if n + 1 < len(au):
                        maxima(n + 1)
                    beside(i, "mla%d" % n)
                    if n >= 1:
                        att_out(n - 1)
                m = 0
                tmp = rg[3]
                for cq in range(2):
                    for br in range(3):
                        for c in range(4):
                            b = bank(dve, i, "bw%d" % br, cq * 4 + c)
                            dve.wait_ge(*at("evicted", i, "gz%d" % br, cq * 4 + c))
                            o = B[:, cq * 4 + c, r]
                            if br == 0:
                                v.tensor_tensor(o, C[:, m % 8, r], b[:, r], ALU.mult).then_inc(
                                    *mark(DVE_EV, ("gated", i, m), ("evicted", i, "bw0", cq * 4 + c)))
                            else:
                                tt = tmp[:, (m % 2) * 512 + r.start:(m % 2) * 512 + r.stop]
                                v.tensor_tensor(tt, C[:, m % 8, r], b[:, r], ALU.mult).then_inc(
                                    *mark(DVE_EV, ("gated", i, m)))
                                dve.wait_ge(*at("gated", i, m))
                                v.tensor_tensor(o, o, tt, ALU.add).then_inc(
                                    *mark(DVE_EV, ("evicted", i, "bw%d" % br, cq * 4 + c)))
                            m += 1
                dve.wait_ge(*at("evicted", *((DEPTH - 1, "mod", 11) if i == 0 else (i, "mod", 11))))
                for c in range(DC):
                    b = bank(dve, i, "y", c)
                    for s in st:
                        x = v.scalar_tensor_tensor(out=XT[:, c, span(s)], in0=b[:, span(s)],
                                                   scalar=mods[:, i, G1 * DC + c, s:s + 1], in1=XT[:, c, span(s)],
                                                   op0=ALU.mult, op1=ALU.add)
                    x.then_inc(*mark(DVE_EV, ("evicted", i, "y", c), ("x1", i, c)))
                dve.wait_ge(*at("x1", i, DC - 1))
                inverse("norm2", i, r)
                dve.wait_ge(*at("amod", i, 1))
                scale_rows("norm2", 1, st)
                u0, q0 = peer_base(i)
                chain = S["dve_topk"]

                def choose(sc0, base, q, qv, par, ahead):
                    n = [0]

                    def step(ins):
                        n[0] += 1
                        ins.then_inc(chain, 1)

                    def settled(alone=False):
                        dve.wait_ge(chain, base + n[0])
                        if alone:
                            dve.sem_inc(S["dve_passed"], 1)
                    step(v.tensor_copy(unit_scores, R[:, bass.ds(sc0, SU)]))
                    settled(True)
                    s = [unit_scores[:, h * PK:h * PK + PK] for h in range(2)]
                    for h in range(2):
                        step(v.max(top1[:, h, 0:8], s[h]))
                    settled(True)
                    for h in range(2):
                        step(v.max_index(topidx[:, h, 0:8], top1[:, h, 0:8], s[h]))
                        step(v.match_replace(sec[:, h, :], top1[:, h, 0:8], s[h], -HUGE))
                    settled(True)
                    for h in range(2):
                        step(v.max(top1[:, h, 8:16], sec[:, h, :]))
                    settled(True)
                    for h in range(2):
                        step(v.max_index(topidx[:, h, 8:16], top1[:, h, 8:16], sec[:, h, :]))
                    step(v.tensor_tensor(cand.rearrange("p (a b) -> p a b", a=PTOP),
                                         top1[:, 0, :].unsqueeze(2).to_broadcast([P, PTOP, PTOP]),
                                         top1[:, 1, :].unsqueeze(1).to_broadcast([P, PTOP, PTOP]), ALU.add))
                    settled(True)
                    step(v.max(top[:, 0:8], cand))
                    step(v.tensor_copy(idxf, topidx[:, :, :].rearrange("p h k -> p (h k)")))
                    settled(True)
                    step(v.max_index(jidx[:, 0:8], top[:, 0:8], cand))
                    step(v.match_replace(cand2, top[:, 0:8], cand, -HUGE))
                    settled(True)
                    step(v.max(top[:, 8:16], cand2))
                    settled(True)
                    step(v.max_index(jidx[:, 8:16], top[:, 8:16], cand2))
                    v.tensor_scalar(shifted, top, top[:, 0:1], None, ALU.subtract).then_inc(S["shift_ready"], 1)
                    settled()
                    step(v.tensor_scalar(jparts[:, 0, :], jidx[:, :], 4, None, ALU.logical_shift_right))
                    step(v.tensor_scalar(jparts[:, 1, :], jidx[:, :], 15, None, ALU.bitwise_and))
                    settled()
                    step(v.tensor_copy(jf, jparts[:, :, :].rearrange("p h k -> p (h k)")))
                    settled()
                    oh = onehot.rearrange("p (s k) -> p s k", k=PTOP)
                    step(v.tensor_tensor(oh, jf.unsqueeze(2).to_broadcast([P, 2 * PTOP, PTOP]),
                                         iota16.unsqueeze(1).to_broadcast([P, 2 * PTOP, PTOP]), ALU.is_equal))
                    settled()
                    oh4 = onehot.rearrange("p (h s k) -> p h s k", h=2, k=PTOP)
                    step(v.tensor_tensor(oh4, oh4, idxf.rearrange("p (h k) -> p h k", h=2).unsqueeze(2).to_broadcast(
                        [P, 2, PTOP, PTOP]), ALU.mult))
                    settled()
                    step(v.tensor_reduce(chosen, oh, AX_X, ALU.add))
                    settled()
                    step(v.tensor_scalar(eidf, chosen[:, 0:PTOP], float(PK), float(i * N_EXP), ALU.mult, ALU.add))
                    settled()
                    v.tensor_tensor(eid[:, par, :], eidf, chosen[:, PTOP:2 * PTOP], ALU.add).then_inc(S["eids_ready"], 1)
                    return n[0]

                def weights(base, qv, par):
                    dve.wait_ge(S["exp_ready"], qv + 1)
                    v.reciprocal(rec[:, 0:1], esum[:, par:par + 1]).then_inc(chain, 1)
                    dve.wait_ge(chain, base + 1)
                    v.tensor_scalar(wts[:, par, :], expd[:, par, :], rec[:, 0:1], None, ALU.mult).then_inc(
                        S["wts_ready"], 1)

                for s in range(0, 8, 2):
                    b = bank(dve, i, "pq", s)
                    copy_out(pqT[:, s, r], b[:, r], i, "pq", s)
                b = bank(dve, i, "ks", tl[0], 0)
                copy_out(R[:, S0:S0 + 512], b[:, :], i, "ks", tl[0], 0)
                dve.wait_ge(*at("evicted", i, "ks", tl[0], 0))
                nsteps = 25
                CH = nsteps + 1
                got = choose(S0, q0 * CH, q0, q0, 0, False)
                assert got == nsteps, got
                for t in tl:
                    b = bank(dve, i, "ht", t, 0)
                    copy_out(GTtok[:, t, 0:512], b[:, :], i, "ht", t, 0)
                for lt, t in enumerate(tl):
                    for g in range(0, 4, 2):
                        if (t, g) != (tl[0], 0):
                            b = bank(dve, i, "ks", t, g)
                            copy_out(R[:, S0 + lt * UNITS * SU + g * 512:S0 + lt * UNITS * SU + g * 512 + 512], b[:, :],
                                     i, "ks", t, g)
                pad = S0 + len(tl) * UNITS * SU
                v.memset(R[:, pad:pad + SU], 0.0).then_inc(*mark("dve_step", ("pad", i)))
                dve.wait_ge(*at("pad", i))
                for g in range(1, 4, 2):
                    for t in tl:
                        dve.wait_ge(*at("evicted", i, "ks", t, g))
                    for t in tl:
                        dve.wait_ge(*at("evicted", i, "ks", t, g - 1))
                for t in tl:
                    dve.wait_ge(*at("evicted", i, "ht", t, 0))
                    dve.wait_ge(*at("evicted", i, "ht", t, 1))
                weights(q0 * CH + nsteps, q0, 0)
                for lt, t in enumerate(tl):
                    with dve.Fori(0, UNITS // 2) as it:
                        for par in range(2):
                            u = lt * UNITS + par
                            for j in range(PTOP):
                                if j == 4:
                                    if u0 + u:
                                        dve.wait_ge(S["diag_ready"], it * (2 * PTOP) + (u0 + u) * PTOP)
                                    choose(it * (2 * SU) + (S0 + (u + 1) * SU), it * (2 * CH) + (q0 + u + 1) * CH, None,
                                           it * 2 + (q0 + u + 1), 1 - par, True)
                                if j == 12:
                                    weights(it * (2 * CH) + ((q0 + u + 1) * CH + nsteps), it * 2 + (q0 + u + 1), 1 - par)
                                dve.wait_ge(gathered[j % RING], it * (2 * 2 * 16) + 16 * (2 * (u0 + u) + j // RING + 1))
                                row = ringslot[j % RING][:, 0:D]
                                v.tensor_tensor_reduce(row, row, GTtok[:, t, :], 1.0, 0.0, ALU.mult, ALU.add,
                                                       dots[:, par, j:j + 1]).then_inc(S["dot_done"], 1)
                    dve.wait_ge(S["row_used"], (u0 + (lt + 1) * UNITS) * PTOP + RING)
                    copy_out(GTtok[:, t, 0:512], ps[bank_no.get((i, "acc", t, 0), 0)][:, :], i, "acc", t, 0)
                    for g in range(2):
                        b = bank(dve, i, "yt", t, g)
                        s = t // 2
                        for c in range(4):
                            cc = g * 4 + c
                            x = v.scalar_tensor_tensor(out=XT[:, cc, tok(t)], in0=b[:, c * P:c * P + P],
                                                       scalar=mods[:, i, G2 * DC + cc, s:s + 1], in1=XT[:, cc, tok(t)],
                                                       op0=ALU.mult, op1=ALU.add)
                        keys = [("evicted", i, "yt", t, g)]
                        if g and t == tl[-1]:
                            keys.append(("x2", i, DC - 1))
                        x.then_inc(*mark(DVE_EV, *keys))
                dve.wait_ge(*at("x2", i, DC - 1))
            i, r = DEPTH - 1, rng(DEPTH - 1)
            inverse("normf", i, r)
            for c in range(DC):
                v.scalar_tensor_tensor(out=HT[:, c, r], in0=XT[:, c, r], scalar=vec[:, V_FG + c:V_FG + c + 1],
                                       in1=scr[:, 2, r], op0=ALU.mult, op1=ALU.mult).then_inc(
                    *mark("dve_step", ("final", c)))

        @block.gpsimd
        def _(pool):
            for i in range(DEPTH):
                tl = tiles(i)
                u0, q0 = peer_base(i)
                for h in range(GLA_H):
                    pool.wait_ge(*at("evicted", i, "k", h))
                for n, (dd, t) in enumerate(gla_units(i)):
                    pool.wait_ge(*at("ekd", i, n))
                    nc.gpsimd.tensor_tensor(gla_buf(n, GD), gla_buf(n, GD), A[:, 4:8, tok(t)], ALU.mult).then_inc(
                        *mark("pool_step", ("gla_kd", i, n)))
                pool.wait_ge(*at("full", i, "ks", TILES - 1, 3))
                if i == 0:
                    pool.sem_inc(S["row_used"], RING)
                for lt, t in enumerate(tl):
                    with pool.Fori(0, UNITS // 2) as it:
                        for par in range(2):
                            u = lt * UNITS + par
                            pool.wait_ge(S["eids_ready"], it * 2 + (q0 + u + 1))
                            for j in range(PTOP):
                                pool.wait_ge(S["row_used"], it * (2 * PTOP) + ((u0 + u) * PTOP + j + 1))
                                pool.sem_inc(S["pool_passed"], 1)
                                pool.indirect_dma_start(ringslot[j % RING], None, d["experts"],
                                                        bass.IndirectOffsetOnAxis(eid[:, par, j:j + 1], 0)).then_inc(
                                    gathered[j % RING], 16)


def constants():
    p = np.arange(P)
    same = (p[:, None] // CHUNK) == (p[None, :] // CHUNK)
    tri = np.stack([same & (p[:, None] <= p[None, :]), same & (p[:, None] >= p[None, :])], 1)
    out = np.zeros((P, C_N), np.float32)
    out[:, C_TRI:C_TRI + 256] = tri.reshape(P, 256)
    out[:, C_ID:C_ID + P] = np.eye(P)
    out[:, C_ONE:C_ONE + P] = 1.0
    out[:, C_DUP:C_DUP + P] = (p[:, None] % ROPE) == (p[None, :] % ROPE)
    half = ROPE // 2
    inv = (10000.0 ** (-np.arange(0, half, 2, dtype=np.float32) / np.float32(half))).astype(np.float32)
    t = np.arange(T_LAT)
    cs = np.zeros((P, T), np.float32)
    cs[0:ROPE, 0:T_CTX] = 1.0
    for part, coord in enumerate((t // GRID_W, t % GRID_W)):
        ang = (coord.astype(np.float32)[None, :] * inv[:, None]).astype(np.float32)
        co, si = np.cos(ang), np.sin(ang)
        a = part * half
        cs[a:a + 16, T_CTX:], cs[a + 16:a + 32, T_CTX:] = co, co
        cs[ROPE + a:ROPE + a + 16, T_CTX:], cs[ROPE + a + 16:ROPE + a + 32, T_CTX:] = -si, si
    out[:, C_CS:C_CS + T] = cs
    out[:, C_IOTA:C_IOTA + 16] = np.arange(16)
    band = np.zeros((len(WINDOWS), 256, 256), np.float32)
    for g, win in enumerate(WINDOWS):
        for j in range(256):
            lo, hi = max(j - win // 2, 0), min(j + win - win // 2, 256)
            band[g, lo:hi, j] = np.float32(1.0) / np.float32(hi - lo)
            band[g, j, j] -= 1.0
    band = band.reshape(len(WINDOWS), 2, P, 256).transpose(2, 0, 1, 3).reshape(P, -1)
    return out, np.ascontiguousarray(band)


def layout(a):
    def cols(v):
        return v.reshape(-1, P).T

    swap = np.concatenate([np.arange(16, 32), np.arange(0, 16), np.arange(48, 64), np.arange(32, 48)])
    w_in = a["w_in"]
    vec = []
    for i in range(DEPTH):
        vec += [cols(a["ada_b"][i]), cols(a["norm1_g"][i]), cols(a["norm2_g"][i]), cols(a["pool_scale"][i]),
                cols(a["mla_q_norm_g"][i]), cols(a["mla_kv_norm_g"][i]), cols(a["gla_norm_g"][i])]
    vec += [cols(a["final_norm_g"]), cols(a["c"][0]), cols(a["c_ctx"])]
    kr = w_in[:, :, 4768:4832]
    uq = a["mla_w_uq"].reshape(DEPTH, QR, MLA_H, NOPE + ROPE)
    uqr = uq[..., NOPE:]
    ukv = a["mla_w_ukv"].reshape(DEPTH, KVR, MLA_H, NOPE + MV)
    const, band = constants()
    out = {
        "const": const, "band": band, "vec": np.concatenate(vec, 1),
        "xT": np.concatenate([a["ctx"][0], a["x"][0]], 0).T,
        "ada_w": a["ada_w"], "w_in": w_in, "w_lr": w_in[:, :, 4096:4128],
        "w_qk": np.concatenate([w_in[:, :, 4128:4512], kr, kr[:, :, swap]], 2),
        "w_kv": w_in[:, :, 4512:4768],
        "gate": np.concatenate([a["gla_gate_w"], a["gla_gate_b"][:, :, None, :]], 2).transpose(0, 2, 1, 3),
        "pool_w": a["pool_w"],
        "w_uqn": uq[..., :NOPE].reshape(DEPTH, QR, -1),
        "w_uqr": np.concatenate([uqr, uqr[..., swap]], -1).reshape(DEPTH, QR, -1),
        "w_ukn": ukv[..., :NOPE].reshape(DEPTH, KVR, -1), "w_ukv": ukv[..., NOPE:].reshape(DEPTH, KVR, -1),
        "branch_w": a["branch_w"], "w_out": a["w_out"], "peer_wq": a["peer_wq"],
        "keys": a["peer_keys"].transpose(0, 4, 2, 1, 3).reshape(DEPTH, PHALF, -1),
        "experts": np.concatenate([a["peer_u"], a["peer_v"]], 2).reshape(DEPTH * N_EXP, 2 * D),
    }
    return {k: np.ascontiguousarray(v) for k, v in out.items()}


def kernel(**inputs):
    import numpy as _np
    import concourse.bacc as _bacc
    from concourse import mybir as _mybir
    from concourse.bass_utils import run_bass_kernel_spmd as _run

    arrays = layout({k: _np.asarray(v) for k, v in inputs.items()})
    count, banks, quads = None, [], []
    for _ in range(2):
        nc = _bacc.Bacc("TRN2", target_bir_lowering=False, num_devices=1)
        dram = {k: nc.dram_tensor("in_" + k, v.shape, _mybir.dt.from_np(v.dtype), kind="ExternalInput").ap()
                for k, v in arrays.items()}
        dram["out"] = nc.dram_tensor("out_0", (D, T_LAT), _mybir.dt.float32, kind="ExternalOutput").ap()
        count = Count(count.table if count else None)
        build(nc, dram, count, banks, quads)
    r = _run(nc, [{"in_" + k: v for k, v in arrays.items()}], core_ids=[0])
    return _np.ascontiguousarray(r.results[0]["out_0"].T).reshape(1, T_LAT, D)
```
